# Optimizing a Trainium2 kernel written in Bass

```python
import math
import jax
import jax.numpy as jnp
from jax import lax
import numpy as np

D_MODEL = 2048
BATCH = 1
SEQ = 128
DEPTH = 1
DEC_BATCH = 1
DEC_SEQ = 256
PAST_LEN = 128

GRID_W = 64
MLA_HEADS = 8
QK_NOPE = 128
QK_ROPE = 64
V_HEAD = 128
Q_LORA = 512
KV_LORA = 256
MLA_WIDTH = MLA_HEADS * V_HEAD
ROPE_THETA = 10000.0
ROPE_FREQS = QK_ROPE // 4
Q_BLOCK = 128
HY_WIDTH = 1024
HY_EMB = 33
HY_BANDS = (HY_EMB - 1) // 2
HY_HIDDEN = 64
HY_FAST_DECAY = 0.3
HY_SLOW_DECAY = 1.5
HY_TARGET = 0.01
N_EXPERTS = 16
EXPERT_FF = 1024
EC_CAPACITY = 2
EPS = 1e-6
ALPHA = (2 * DEPTH) ** 0.25
BETA = (8 * DEPTH) ** -0.25
N_MOD = 6
IN_SPLITS = (Q_LORA,
             Q_LORA + KV_LORA,
             Q_LORA + KV_LORA + QK_ROPE,
             Q_LORA + KV_LORA + QK_ROPE + 3 * HY_WIDTH,
             Q_LORA + KV_LORA + QK_ROPE + 3 * HY_WIDTH + D_MODEL)
IN_WIDTH = IN_SPLITS[-1] + D_MODEL

kernel_name = 'hybrid_mla_hyena_ec_diffusion_step'

def layer_norm(x, g, b):
    xf = x.astype(jnp.float32)
    mu = jnp.mean(xf, axis=-1, keepdims=True)
    var = jnp.mean(jnp.square(xf - mu), axis=-1, keepdims=True)
    y = (xf - mu) * lax.rsqrt(var + EPS) * g.astype(jnp.float32) + b.astype(jnp.float32)
    return y.astype(x.dtype)

def rms_norm(x, g):
    xf = x.astype(jnp.float32)
    y = xf * lax.rsqrt(jnp.mean(jnp.square(xf), axis=-1, keepdims=True) + EPS) * g.astype(jnp.float32)
    return y.astype(x.dtype)

def adaln_mod(cond, w_ada, b_ada):
    mod = (jax.nn.silu(cond) @ w_ada + b_ada)[..., None, :]
    return jnp.split(mod, N_MOD, axis=-1)

def axial_rope_tables(n_tokens, dtype):
    n_rows = n_tokens // GRID_W
    row = jnp.repeat(jnp.arange(n_rows, dtype=jnp.float32), GRID_W)
    col = jnp.tile(jnp.arange(GRID_W, dtype=jnp.float32), n_rows)
    inv = ROPE_THETA ** (-jnp.arange(ROPE_FREQS, dtype=jnp.float32) / ROPE_FREQS)
    ang = jnp.stack([row[:, None] * inv, col[:, None] * inv], axis=1)
    return jnp.cos(ang).astype(dtype), jnp.sin(ang).astype(dtype)

def apply_axial_rope(x, cos, sin):
    xs = x.reshape(x.shape[:-1] + (2, 2, ROPE_FREQS))
    a, b = xs[..., 0, :], xs[..., 1, :]
    out = jnp.stack([a * cos - b * sin, b * cos + a * sin], axis=-2)
    return out.reshape(x.shape)

def mla_attention(q_nope, q_rope, k_nope, k_rope, v):
    B, Lq, H, _ = q_nope.shape
    nb = Lq // Q_BLOCK
    scale = (QK_NOPE + QK_ROPE) ** -0.5
    qn = q_nope.reshape(B, nb, Q_BLOCK, H, QK_NOPE).transpose(1, 0, 2, 3, 4)
    qr = q_rope.reshape(B, nb, Q_BLOCK, H, QK_ROPE).transpose(1, 0, 2, 3, 4)

    def block(args):
        qn_b, qr_b = args
        s = (jnp.einsum('bqhd,bkhd->bhqk', qn_b, k_nope)
             + jnp.einsum('bqhr,bkr->bhqk', qr_b, k_rope))
        p = jax.nn.softmax(s.astype(jnp.float32) * scale, axis=-1).astype(v.dtype)
        return jnp.einsum('bhqk,bkhd->bqhd', p, v)

    o = lax.map(block, (qn, qr))
    return o.transpose(1, 0, 2, 3, 4).reshape(B, Lq, H * V_HEAD)

def short_conv3(u, w, b):
    up = jnp.pad(u, ((0, 0), (1, 1), (0, 0)))
    return up[:, :-2] * w[0] + up[:, 1:-1] * w[1] + up[:, 2:] * w[2] + b

def implicit_filter(L, p):
    f32 = lambda a: a.astype(jnp.float32)
    pos = jnp.arange(L, dtype=jnp.float32)
    t = pos / max(L - 1, 1)
    bands = jnp.linspace(1e-4, HY_BANDS - 1, HY_BANDS, dtype=jnp.float32)
    w = 2.0 * math.pi * pos / L
    feats = jnp.concatenate([t[:, None], jnp.cos(w[:, None] * bands), -jnp.sin(w[:, None] * bands)], axis=-1)
    hdn = jnp.sin(f32(p['hy_filt_freq1']) * (feats @ f32(p['hy_filt_w1']) + f32(p['hy_filt_b1'])))
    hdn = jnp.sin(f32(p['hy_filt_freq2']) * (hdn @ f32(p['hy_filt_w2']) + f32(p['hy_filt_b2'])))
    h = hdn @ f32(p['hy_filt_w3']) + f32(p['hy_filt_b3'])
    deltas = jnp.abs(jnp.linspace(math.log(HY_TARGET) / HY_SLOW_DECAY, math.log(HY_TARGET) / HY_FAST_DECAY,
                                  HY_WIDTH, dtype=jnp.float32))
    window = jnp.exp(-t[:, None] * deltas)
    h_fwd = h[:, :HY_WIDTH] * window
    h_bwd = h[:, HY_WIDTH:] * window
    kernel = jnp.concatenate([h_fwd, jnp.zeros((1, HY_WIDTH), jnp.float32), h_bwd[:0:-1]], axis=0)
    return kernel / (jnp.sum(jnp.abs(kernel), axis=0, keepdims=True) + EPS)

def fft_long_conv(z, kernel):
    L = z.shape[1]
    zf = jnp.fft.rfft(z.astype(jnp.float32), n=2 * L, axis=1)
    kf = jnp.fft.rfft(kernel, n=2 * L, axis=0)
    return jnp.fft.irfft(zf * kf[None], n=2 * L, axis=1)[:, :L].astype(z.dtype)

def hyena_branch(u_proj, p):
    u = short_conv3(u_proj, p['hy_short_w'], p['hy_short_b'])
    x0, x1, v = jnp.split(u, 3, axis=-1)
    z = x1 * v
    kernel = implicit_filter(u.shape[1], p)
    y = fft_long_conv(z, kernel) + z * p['hy_skip']
    return x0 * y

def token_mixer(h, p, ctx_kv_c, ctx_k_rope):
    B, L, _ = h.shape
    proj = h @ p['w_in']
    q_c, kv_c, k_r, hy_in, g_a, g_b = jnp.split(proj, IN_SPLITS, axis=-1)
    q = (rms_norm(q_c, p['q_norm_g']) @ p['w_uq']).reshape(B, L, MLA_HEADS, QK_NOPE + QK_ROPE)
    q_nope, q_rope = q[..., :QK_NOPE], q[..., QK_NOPE:]
    c_kv = rms_norm(kv_c, p['kv_norm_g'])
    if ctx_kv_c is None:
        k_rope = k_r
        kv_all, kr_all = c_kv, k_rope
    else:
        cos, sin = axial_rope_tables(L, h.dtype)
        q_rope = apply_axial_rope(q_rope, cos[:, None], sin[:, None])
        k_rope = apply_axial_rope(k_r, cos, sin)
        kv_all = jnp.concatenate([ctx_kv_c, c_kv], axis=1)
        kr_all = jnp.concatenate([ctx_k_rope, k_rope], axis=1)
    kv = (kv_all @ p['w_ukv']).reshape(B, kv_all.shape[1], MLA_HEADS, QK_NOPE + V_HEAD)
    attn = mla_attention(q_nope, q_rope, kv[..., :QK_NOPE], kr_all, kv[..., QK_NOPE:])
    hy = hyena_branch(hy_in, p)
    merged = jax.nn.sigmoid(g_a) * (attn @ p['w_o_mla']) + jax.nn.sigmoid(g_b) * (hy @ p['w_o_hy'])
    return merged @ p['w_out'], c_kv, k_rope

def expert_choice_ffn(h, p):
    B, L, D = h.shape
    tok = h.reshape(B * L, D)
    cap = EC_CAPACITY * (B * L) // N_EXPERTS
    aff = jax.nn.softmax((tok @ p['w_router']).astype(jnp.float32), axis=-1)
    gate, idx = lax.top_k(aff.T, cap)
    xe = tok[idx]
    hid = jax.nn.silu(jnp.einsum('ecd,edf->ecf', xe, p['w_gate'])) * jnp.einsum('ecd,edf->ecf', xe, p['w_up'])
    ye = jnp.einsum('ecf,efd->ecd', hid, p['w_down']) * gate[..., None].astype(tok.dtype)
    out = jnp.zeros_like(tok).at[idx.reshape(-1)].add(ye.reshape(-1, D))
    return out.reshape(B, L, D)

def trunk_layer(x, mods, p, ctx_kv_c, ctx_k_rope):
    shift1, scale1, gate1, shift2, scale2, gate2 = mods
    mix, c_kv, k_rope = token_mixer(x * (1 + scale1) + shift1, p, ctx_kv_c, ctx_k_rope)
    x = layer_norm(ALPHA * x + gate1 * mix, p['ln1_g'], p['ln1_b'])
    ffn = expert_choice_ffn(x * (1 + scale2) + shift2, p)
    x = layer_norm(ALPHA * x + gate2 * ffn, p['ln2_g'], p['ln2_b'])
    return x, c_kv, k_rope

def setup_inputs(seed: int = 0) -> dict:
    key = jax.random.key(seed)
    keys = iter(jax.random.split(key, 64))

    def nrm(shape, std):
        return jax.random.normal(next(keys), shape, jnp.float32) * std

    def gain(shape):
        return 1.0 + nrm(shape, 0.02)

    hy3 = 3 * HY_WIDTH
    return {
        'x_prompt': nrm((BATCH, SEQ, D_MODEL), 1.0),
        'x_sample': nrm((DEC_BATCH, DEC_SEQ, D_MODEL), 1.0),
        'cache_kv_c': nrm((DEC_BATCH, DEPTH, PAST_LEN, KV_LORA), 1.0),
        'cache_k_rope': nrm((DEC_BATCH, DEPTH, PAST_LEN, QK_ROPE), 1.0),
        'c': nrm((DEC_BATCH, D_MODEL), 1.0),
        'c_ctx': nrm((D_MODEL,), 1.0),
        'w_ada': nrm((DEPTH, D_MODEL, N_MOD * D_MODEL), D_MODEL ** -0.5),
        'b_ada': nrm((DEPTH, N_MOD * D_MODEL), 0.02),
        'w_in': nrm((DEPTH, D_MODEL, IN_WIDTH), D_MODEL ** -0.5),
        'q_norm_g': gain((DEPTH, Q_LORA)),
        'kv_norm_g': gain((DEPTH, KV_LORA)),
        'w_uq': nrm((DEPTH, Q_LORA, MLA_HEADS * (QK_NOPE + QK_ROPE)), Q_LORA ** -0.5),
        'w_ukv': nrm((DEPTH, KV_LORA, MLA_HEADS * (QK_NOPE + V_HEAD)), KV_LORA ** -0.5),
        'w_o_mla': nrm((DEPTH, MLA_WIDTH, D_MODEL), MLA_WIDTH ** -0.5),
        'hy_short_w': nrm((DEPTH, 3, hy3), 3 ** -0.5),
        'hy_short_b': nrm((DEPTH, hy3), 0.02),
        'hy_filt_w1': nrm((DEPTH, HY_EMB, HY_HIDDEN), HY_EMB ** -0.5),
        'hy_filt_b1': nrm((DEPTH, HY_HIDDEN), 0.02),
        'hy_filt_freq1': gain((DEPTH, HY_HIDDEN)),
        'hy_filt_w2': nrm((DEPTH, HY_HIDDEN, HY_HIDDEN), HY_HIDDEN ** -0.5),
        'hy_filt_b2': nrm((DEPTH, HY_HIDDEN), 0.02),
        'hy_filt_freq2': gain((DEPTH, HY_HIDDEN)),
        'hy_filt_w3': nrm((DEPTH, HY_HIDDEN, 2 * HY_WIDTH), HY_HIDDEN ** -0.5),
        'hy_filt_b3': nrm((DEPTH, 2 * HY_WIDTH), 0.02),
        'hy_skip': nrm((DEPTH, HY_WIDTH), 0.5),
        'w_o_hy': nrm((DEPTH, HY_WIDTH, D_MODEL), HY_WIDTH ** -0.5),
        'w_out': nrm((DEPTH, D_MODEL, D_MODEL), BETA * D_MODEL ** -0.5),
        'ln1_g': gain((DEPTH, D_MODEL)),
        'ln1_b': nrm((DEPTH, D_MODEL), 0.02),
        'ln2_g': gain((DEPTH, D_MODEL)),
        'ln2_b': nrm((DEPTH, D_MODEL), 0.02),
        'w_router': nrm((DEPTH, D_MODEL, N_EXPERTS), D_MODEL ** -0.5),
        'w_gate': nrm((DEPTH, N_EXPERTS, D_MODEL, EXPERT_FF), D_MODEL ** -0.5),
        'w_up': nrm((DEPTH, N_EXPERTS, D_MODEL, EXPERT_FF), D_MODEL ** -0.5),
        'w_down': nrm((DEPTH, N_EXPERTS, EXPERT_FF, D_MODEL), BETA * EXPERT_FF ** -0.5),
    }

def reference(x_prompt, x_sample, cache_kv_c, cache_k_rope, c, c_ctx, w_ada, b_ada, w_in,
              q_norm_g, kv_norm_g, w_uq, w_ukv, w_o_mla, hy_short_w, hy_short_b,
              hy_filt_w1, hy_filt_b1, hy_filt_freq1, hy_filt_w2, hy_filt_b2, hy_filt_freq2,
              hy_filt_w3, hy_filt_b3, hy_skip, w_o_hy, w_out, ln1_g, ln1_b, ln2_g, ln2_b,
              w_router, w_gate, w_up, w_down):
    y_prompt = x_prompt
    y_sample = x_sample
    kv_list = []
    kr_list = []
    for l in range(DEPTH):
        p = {
            'w_in': w_in[l], 'q_norm_g': q_norm_g[l], 'kv_norm_g': kv_norm_g[l],
            'w_uq': w_uq[l], 'w_ukv': w_ukv[l], 'w_o_mla': w_o_mla[l],
            'hy_short_w': hy_short_w[l], 'hy_short_b': hy_short_b[l],
            'hy_filt_w1': hy_filt_w1[l], 'hy_filt_b1': hy_filt_b1[l], 'hy_filt_freq1': hy_filt_freq1[l],
            'hy_filt_w2': hy_filt_w2[l], 'hy_filt_b2': hy_filt_b2[l], 'hy_filt_freq2': hy_filt_freq2[l],
            'hy_filt_w3': hy_filt_w3[l], 'hy_filt_b3': hy_filt_b3[l], 'hy_skip': hy_skip[l],
            'w_o_hy': w_o_hy[l], 'w_out': w_out[l],
            'ln1_g': ln1_g[l], 'ln1_b': ln1_b[l], 'ln2_g': ln2_g[l], 'ln2_b': ln2_b[l],
            'w_router': w_router[l], 'w_gate': w_gate[l], 'w_up': w_up[l], 'w_down': w_down[l],
        }
        mods_ctx = adaln_mod(c_ctx, w_ada[l], b_ada[l])
        y_prompt, c_kv, k_rope = trunk_layer(y_prompt, mods_ctx, p, None, None)
        kv_list.append(c_kv)
        kr_list.append(k_rope)
        mods_lat = adaln_mod(c, w_ada[l], b_ada[l])
        y_sample, _, _ = trunk_layer(y_sample, mods_lat, p, cache_kv_c[:, l], cache_k_rope[:, l])
    new_kv_c = jnp.stack(kv_list, axis=1)
    new_k_rope = jnp.stack(kr_list, axis=1)
    return (y_prompt, y_sample, new_kv_c, new_k_rope)


_drawn_inputs = setup_inputs


def setup_inputs(seed=0):
    import zlib

    import numpy as np

    out = dict(_drawn_inputs(seed))
    spreads = {}
    factors = {'cache_kv_c': 5.23,
     'cache_k_rope': 8.0,
     'b_ada': 2.705,
     'q_norm_g': 8.0,
     'w_uq': 2.746,
     'hy_short_b': 5.833,
     'hy_filt_b1': 8.0,
     'hy_filt_freq1': 8.0,
     'hy_filt_b2': 8.0,
     'hy_filt_freq2': 50.673,
     'hy_filt_b3': 23.443,
     'ln2_g': 8.101,
     'ln2_b': 7.882}
    for name, (base, spread) in spreads.items():
        noise = np.random.default_rng([zlib.crc32(name.encode()), seed]).standard_normal(out[name].shape)
        drawn = base * np.exp(spread * noise) if base else spread * noise
        out[name] = jnp.asarray(drawn.astype(out[name].dtype))
    for name, factor in factors.items():
        out[name] = (out[name] * factor).astype(out[name].dtype)
    return out
```

```python
from contextlib import ExitStack
import math

import concourse.bass as bass
from concourse import mybir

F32 = mybir.dt.float32
ALU = mybir.AluOpType
ACT = mybir.ActivationFunctionType
AX_X = mybir.AxisListType.X

P = 128
D = 2048
LC, LS = 128, 256
NT = LC + LS
PAST = 128
KD = D // P
GROUPS = ((0, 0, LC), (1, LC, NT))
H, NOPE, ROPE, VH = 8, 128, 64, 128
QL, KVL = 512, 256
HY = 1024
NE, FF = 16, 1024
CAP_C, CAP_S = 2 * LC // NE, 2 * LS // NE
EPS = 1e-6
ALPHA = 2.0 ** 0.25
EMB, HID = 33, 64
SCALE = (NOPE + ROPE) ** -0.5
COL_KV, COL_KR, COL_HY = QL, QL + KVL, QL + KVL + ROPE
COL_GA = COL_HY + 3 * HY
COL_GB = COL_GA + D
TWO_PI_HI = 6.28125
TWO_PI_MID = 0.001934051513671875
TWO_PI_LO = 2.0 * math.pi - TWO_PI_HI - TWO_PI_MID
ROUND = 12582912.0

SCATTER_BANKS = (5, 6, 7, 0, 1, 2)
RING, SLOT = 6, 4096


def prefix_stream():
    out = [("ada", m, k) for m in (0, 1) for k in range(8)]
    ada2 = [("ada", 2, k) for k in range(8)]
    for item in (("q", 0, 0), ("q", 1, 0), ("kv", 0, 0), ("kr", 0, 0)):
        out.append(item)
        out += [ada2.pop(0), ada2.pop(0)]
    out += [("uq", 0, 0), ("uq", 1, 0), ("ukv", 0, 0)]
    rest = [("ada", m, k) for m in (3, 4, 5) for k in range(8)]
    for c in range(4):
        for part in (1, 2, 0):
            out.append(("hy", part, c))
            out += [rest.pop(0), rest.pop(0)]
    return out


def build(nc, t, consts, outs, mods_dram):
    stream = prefix_stream()
    N_PRE = len(stream)
    N_OUT = N_PRE + 24
    N_EXP = N_OUT + 8
    y_prompt, y_sample, new_kv, new_kr = outs

    with ExitStack() as ctx:
        def sem(name):
            return ctx.enter_context(nc.semaphore(name))

        ring = ctx.enter_context(nc.sbuf_tensor("ring", [P, RING, SLOT], F32))
        arena = ctx.enter_context(nc.sbuf_tensor("arena", [P, 28600], F32))
        ps = [ctx.enter_context(nc.psum_tensor(f"ps{i}", [P, 512], F32)) for i in range(8)]

        def view(off, *dims, parts=P):
            n = math.prod(dims)
            ap = arena[0:parts, off:off + n]
            if len(dims) == 1:
                return ap
            names = "abcd"[:len(dims)]
            return ap.rearrange("p (%s) -> p %s" % (" ".join(names), " ".join(names)),
                                **{c: d for c, d in zip(names, dims)})

        A_HT, A_MG, A_ACC, A_R = 0, 6144, 12288, 18432
        hT = view(A_HT, KD, NT)
        h2 = view(A_HT, 3, D)
        wtmp = view(A_HT, 4, 256)
        mergedT = view(A_MG, KD, NT)
        vals = view(A_MG, 4, H * VH)
        kv_junk = view(A_R + 1796 + 7760, 256)
        kvT = view(A_MG + 4096, 2, 512)
        kT = view(A_MG + 5120, 2, 512)
        zT = view(A_MG, 8, NT)
        z_tok = view(A_MG + 3072, 3, 512)
        window = view(A_MG + 4608, 3, 512)
        x1T = view(A_MG + 3072, 2, NT)
        mod_s = view(A_MG, 2, D)
        h2T = view(A_MG, KD, NT)
        ln2 = view(A_MG, 2, D)
        acc = view(A_ACC, 3, D)
        attT = view(A_ACC, 8, NT)
        x0T = view(A_ACC + 3072, 8, NT)
        qN = view(A_ACC + 3072, 8, NT)

        o = A_R
        K_W = 546
        ident = view(o, P)
        perm = view(o + 128, P)
        tri = view(o + 256, P)
        iota = view(o + 384, 32)
        bmask = view(o + 416, 1)
        ones = view(o + 417, 1)
        rope_k = view(o + 418, 2, 2, 32)
        kconst = view(o, K_W)
        cols = view(o + 546, 108)
        q_g = view(o + 546, 4)
        sw = view(o + 550, 3, 24)
        sb_ = view(o + 622, 24)
        skip = view(o + 646, 8)
        condT = view(o + 654, 2, KD)
        modc = view(o + 686, 2, 2, KD)
        fcol = view(o + 750, 4)
        rnorm = view(o + 754, 2, 8)
        rq = view(o + 770, 3)
        smx = view(o + 773, 2, 3)
        snb = view(o + 779, 2, 3)
        srs = view(o + 785, 2, 3)
        srr = view(o + 791, 2, 3)
        stat = view(o + 797, 24)
        mv = view(o + 821, 2)
        rstd = view(o + 823, 2)
        ss_kv = view(o + 826, 3)
        r_kv = view(o + 829, 3)
        nsum = view(o + 832, 8)
        stage = view(o + 900, 512)
        w_router = view(o + 900, KD, NE)
        hdn = view(o + 1412, NT, parts=HID + 1)
        Y = o + 1796

        vec_rows = view(Y, P, parts=108)
        c_rows = view(Y + 128, P, parts=32)
        feats = view(Y + 256, NT, parts=EMB)
        fw1 = view(Y + 640, HID, parts=EMB)
        fw2 = view(Y + 704, HID, parts=HID)
        farg = view(Y + 768, NT, parts=HID)
        frnd = view(Y + 1152, NT, parts=HID)
        fh1 = view(Y + 1536, NT, parts=HID)
        qR = view(Y, 4, NT)
        krT = view(Y + 1536, 512)
        qc = view(Y + 2048, 4, NT)
        qsq = view(Y + 3584, 4, NT)
        rope_q = view(Y + 5120, 2, LS)
        prob = view(Y + 2048, 2, 896)
        probT = view(Y + 3840, 2, 896)
        ckv = view(Y + 5632, 4, KVL)
        kr = view(Y + 6656, 4, 2 * ROPE)
        kv_g = view(Y + 7168, KVL)
        rtmp = view(Y + 7424, LS)
        ktmp = view(Y + 7680, 2, 32)
        kA = view(Y, 2, 512)
        kB = view(Y + 1024, 2, 512)
        spP = view(Y, 2, 512)
        spQ = view(Y + 1024, 2, 512)
        kSr = view(Y + 2048, 2, 512)
        kSs = view(Y + 3072, 2, 512)
        f256 = view(Y + 4096, 2, 2, LS)
        f128 = view(Y + 5120, 2, LC)
        i256 = view(Y + 5376, 2, 2, LS)
        i128 = view(Y + 6400, 2, LC)
        dft = view(Y + 4096, 2560)
        w3 = view(Y + 6656, 2, 512, parts=HID + 1)
        ktmp2 = view(Y + 7680, 512)
        sig = view(Y, 2, 2, NT)
        gsum = view(Y + 4 * NT, 2, NT)
        gate1 = view(Y, 2, D)
        ln1 = view(Y + 4096, 2, D)
        mod_c = view(Y, 2, D)
        aff = view(Y, 3, NE)
        lsm = view(Y + 48, 3, 4)
        logits = view(Y + 820, 3 * NE)
        affT = view(Y + 64, NT, parts=NE)
        junk = view(Y + 448, LS)
        cnt = view(Y + 704, 7, NE)
        route = view(Y + 5368 + 1024, NE + 1, 6)
        cur = view(Y + 906, 2, 6)
        pick = view(Y + 920, 3, 32)
        give = view(Y + 1016, 3, P)
        xe = view(Y + 1400, KD, 64)
        comb = view(Y + 2424, 3, P)
        sil = view(Y + 2808, 512)
        hid = view(Y + 3320, 512)
        hidT = view(Y + 3832, 4, P)
        ye = view(Y + 4344, 2, 512)
        g2 = view(Y + 5368, 2, 512)

        full = [sem(f"slot_full{s}") for s in range(RING)]
        used = [sem(f"slot_used{s}") for s in range(RING)]
        ld_const, ld_vec, ld_c, ld_filt, ld_x = map(sem, ("ld_const", "ld_vec", "ld_c", "ld_filt", "ld_x"))
        ld_bada, ld_att, ld_dft, ld_w3, ld_w3b = map(sem, ("ld_bada", "ld_att", "ld_dft", "ld_w3", "ld_w3b"))
        ld_x2, ld_g1, ld_ln1, ld_modc, ld_mods, ld_wr = map(sem, ("ld_x2", "ld_g1", "ld_ln1", "ld_modc", "ld_mods", "ld_wr"))
        ld_g2, ld_ln2, st_mods, st_out, st_kv = map(sem, ("ld_g2", "ld_ln2", "st_mods", "st_out", "st_kv"))
        dv, av, gp = sem("dve_chain"), sem("act_chain"), sem("pool_chain")
        names = ("silu_done condT_ps condT_done vec_ps vec_done xT_ps xT_done filt_ps farg_done sin_done "
                 "ada_rows col_ps col_done mod_lat mod_ctx q_done qsq_done qsum_ps kv_sq kv_var kv_std kv_tok "
                 "q_var q_std rq_done kvT_ps kvT_done uq_ps uq_done rot_ps rot_done kT_ps kT_done val_ps val_done "
                 "sc_ps nb_done exp_done prob_done pT_ps pT_done av_ps av_done "
                 "hy_mid hy_done zt_ps zt_done kp_ps kab_done kn_ps kn_done kf_ps kf_done zf_ps pq_done "
                 "yT_ps hyT_done sig_a sig_b mrg_done wo_done var_done std_done "
                 "x1_done h2_done h2T_ps h2T_done lg_ps lmx_done lexp_done aff_done affT_ps affT_done br_ps br_used "
                 "pick_done give_done xe_ps xe_d xe_a comb_ps comb_done sil_done hid_done hT_ps hT_done "
                 "ye_done cb_ps cb_used ones_done zero_done out_ready").split()
        S = {n: sem(n) for n in names}

        def n_dmas(n):
            return 2 if N_PRE <= n < N_OUT and (n - N_PRE) % 3 == 2 else 1

        filled = {}
        tally = [0] * RING
        for n in range(N_EXP):
            tally[n % RING] += 16 * n_dmas(n)
            filled[n] = tally[n % RING]
        exp_fill0 = list(tally)
        per_turn = [0] * RING
        for n in range(N_PRE, N_PRE + 6):
            per_turn[n % RING] += 16 * n_dmas(n)

        def slot(n, *dims):
            ap = ring[:, n % RING, 0:math.prod(dims)]
            names_ = "abcd"[:len(dims)]
            return ap.rearrange("p (%s) -> p %s" % (" ".join(names_), " ".join(names_)),
                                **{c: d for c, d in zip(names_, dims)})

        class Chain:
            def __init__(self, eng, s):
                self.eng, self.s, self.n, self.base = eng, s, 0, 0

            def inc(self, ins):
                self.n += 1
                ins.then_inc(self.s, 1)

            def wait(self):
                self.eng.wait_ge(self.s, self.base + self.n)

            def link(self, ins):
                self.inc(ins)
                self.wait()

        def through(eng, n):
            eng.wait_ge(used[n % RING], n // RING + 1)

        w_in_v = t["w_in"][0].rearrange("(k p) n -> p k n", p=P)
        w_ada_v = t["w_ada"][0].rearrange("(k p) n -> p k n", p=P)
        w_uq_v = t["w_uq"][0].rearrange("(k p) n -> p k n", p=P)
        w_ukv_v = t["w_ukv"][0].rearrange("(k p) n -> p k n", p=P)
        w_oa_v = t["w_o_mla"][0].rearrange("(k p) n -> p k n", p=P)
        w_oh_v = t["w_o_hy"][0].rearrange("(k p) n -> p k n", p=P)
        w_out_v = t["w_out"][0].rearrange("(k p) n -> p k n", p=P)
        w_gate_v = t["w_gate"].rearrange("o e (k p) n -> p (o e) k n", p=P)
        w_up_v = t["w_up"].rearrange("o e (k p) n -> p (o e) k n", p=P)
        w_down_v = t["w_down"].rearrange("o e (k p) n -> p (o e) k n", p=P)
        hy_col = lambda part, c: COL_HY + part * HY + c * 256

        block = ctx.enter_context(nc.Block())

        @block.sync
        def _(sp):
            for n, (kind, a, b) in enumerate(stream):
                if n >= RING:
                    sp.wait_ge(used[n % RING], n // RING)
                if kind == "ada":
                    dst, src = slot(n, 2, D), w_ada_v[:, 2 * b:2 * b + 2, a * D:(a + 1) * D]
                elif kind == "q":
                    dst, src = slot(n, KD, 256), w_in_v[:, :, a * 256:(a + 1) * 256]
                elif kind == "kv":
                    dst, src = slot(n, KD, KVL), w_in_v[:, :, COL_KV:COL_KR]
                elif kind == "kr":
                    dst, src = slot(n, KD, ROPE), w_in_v[:, :, COL_KR:COL_HY]
                elif kind == "uq":
                    dst, src = slot(n, 4, 768), w_uq_v[:, :, a * 768:(a + 1) * 768]
                elif kind == "ukv":
                    dst, src = slot(n, 2, D), w_ukv_v
                else:
                    c0 = hy_col(a, b)
                    dst, src = slot(n, KD, 256), w_in_v[:, :, c0:c0 + 256]
                sp.dma_start(dst, src).then_inc(full[n % RING], 16)
            with sp.Fori(0, 4) as i:
                for sub in range(2):
                    for j in range(3):
                        n = N_PRE + 3 * sub + j
                        s = n % RING
                        c0 = i * 512 + sub * 256 + (COL_GA, COL_GB, 0)[j]
                        sp.wait_ge(used[s], n // RING)
                        sp.wait_ge(used[s], n // RING + i)
                        if j < 2:
                            sp.dma_start(slot(n, KD, 256), w_in_v[:, :, bass.ds(c0, 256)]).then_inc(full[s], 16)
                        else:
                            for half, w in enumerate((w_oa_v, w_oh_v)):
                                sp.dma_start(slot(n, 2, 8, 256)[:, half], w[:, :, bass.ds(c0, 256)])\
                                  .then_inc(full[s], 16)
            for j in range(8):
                n = N_OUT + j
                sp.wait_ge(used[n % RING], n // RING)
                sp.dma_start(slot(n, KD, 256), w_out_v[:, :, j * 256:(j + 1) * 256]).then_inc(full[n % RING], 16)
            with sp.Fori(0, NE) as e:
                for j in range(12):
                    n = N_EXP + j
                    s = n % RING
                    sp.wait_ge(used[s], n // RING)
                    sp.wait_ge(used[s], n // RING + e * 2)
                    if j < 8:
                        w, k0 = (w_gate_v, w_up_v)[j // 4], 4 * (j % 4)
                        src = w[:, bass.ds(e, 1), k0:k0 + 4, :].rearrange("p e k n -> p (e k) n")
                        sp.dma_start(slot(n, 4, FF), src).then_inc(full[s], 16)
                    else:
                        k0 = 2 * (j - 8)
                        src = w_down_v[:, bass.ds(e, 1), k0:k0 + 2, :].rearrange("p e k n -> p (e k) n")
                        sp.dma_start(slot(n, 2, D), src).then_inc(full[s], 16)
            sp.wait_ge(S["out_ready"], 3)
            sp.dma_start(y_prompt[0], acc[:, 0, :]).then_inc(st_out, 16)
            sp.dma_start(y_sample[0].rearrange("(a p) n -> p a n", p=P), acc[:, 1:3, :]).then_inc(st_out, 16)
            sp.wait_ge(st_out, 32)
            sp.wait_ge(st_kv, 32)
            sp.wait_ge(st_mods, 256)

        @block.gpsimd
        def _(pool):
            def row(ap, parts):
                return ap.partition_broadcast(parts)

            pool.dma_start(kconst, consts["kconst"]).then_inc(ld_const, 16)
            pool.dma_start(c_rows[0:KD], t["c_ctx"].rearrange("(b p) -> b p", p=P)).then_inc(ld_c, 16)
            pool.dma_start(c_rows[KD:2 * KD], t["c"][0].rearrange("(b p) -> b p", p=P)).then_inc(ld_c, 16)
            pool.dma_start(vec_rows[0:4], t["q_norm_g"][0].rearrange("(b p) -> b p", p=P)).then_inc(ld_vec, 16)
            pool.dma_start(vec_rows[4:76], t["hy_short_w"][0].rearrange("a (b p) -> (a b) p", p=P)).then_inc(ld_vec, 16)
            pool.dma_start(vec_rows[76:100], t["hy_short_b"][0].rearrange("(b p) -> b p", p=P)).then_inc(ld_vec, 16)
            pool.dma_start(vec_rows[100:108], t["hy_skip"][0].rearrange("(b p) -> b p", p=P)).then_inc(ld_vec, 16)
            pool.dma_start(feats, consts["feats"]).then_inc(ld_filt, 16)
            pool.dma_start(fw1, t["hy_filt_w1"][0]).then_inc(ld_filt, 16)
            pool.dma_start(fw2, t["hy_filt_w2"][0]).then_inc(ld_filt, 16)
            for n, name in enumerate(("b1", "freq1", "b2", "freq2")):
                pool.dma_start(fcol[0:HID, n:n + 1], t["hy_filt_" + name][0].rearrange("(a b) -> a b", b=1))\
                    .then_inc(ld_filt, 16)
            pool.memset(hdn[HID:HID + 1, :], 1.0).then_inc(S["ones_done"], 1)

            def load_bada(m):
                for g in range(4):
                    c0 = m * D + g * 512
                    pool.dma_start(stage[32 * g:32 * g + 2, :], row(t["b_ada"][0, c0:c0 + 512], 2)).then_inc(ld_bada, 16)

            load_bada(0)
            pool.wait_ge(S["col_ps"], 1)
            load_bada(1)
            pool.wait_ge(S["col_ps"], 2)
            load_bada(2)
            pool.wait_ge(S["sin_done"], 2)
            pool.wait_ge(S["filt_ps"], 2)
            pool.dma_start(ckv[:, 1, :], t["cache_kv_c"][0, 0]).then_inc(ld_att, 16)
            pool.dma_start(kr[:, 1, 0:ROPE], t["cache_k_rope"][0, 0]).then_inc(ld_att, 16)
            pool.dma_start(kr[:, 1, ROPE:2 * ROPE], t["cache_k_rope"][0, 0]).then_inc(ld_att, 16)
            pool.dma_start(kv_g, row(t["kv_norm_g"][0], P)).then_inc(ld_att, 16)
            pool.dma_start(rope_q, consts["rope_q"]).then_inc(ld_att, 16)
            pool.wait_ge(S["kv_tok"], 3)
            pool.dma_start(new_kv[0, 0], ckv[:, 0, :]).then_inc(st_kv, 16)
            pool.dma_start(new_kr[0, 0], kr[:, 0, 0:ROPE]).then_inc(st_kv, 16)

            def store_mods(m):
                pool.wait_ge(S["ada_rows"], m + 1)
                for g in range(4):
                    pool.dma_start(mods_dram[m - 2, :, g * 512:(g + 1) * 512], stage[32 * g:32 * g + 2, :])\
                        .then_inc(st_mods, 16)
                pool.wait_ge(st_mods, 64 * (m - 1))

            store_mods(2)
            load_bada(3)
            pool.wait_ge(S["av_ps"], H)
            pool.wait_ge(st_kv, 32)
            pool.dma_start(dft, consts["dft"]).then_inc(ld_dft, 16)

            def load_w3(c, s):
                w = t["hy_filt_w3"][0].rearrange("h (d n) -> h d n", d=2)
                b = t["hy_filt_b3"].rearrange("o (d n) -> o d n", d=2)
                pool.dma_start(w3[0:HID], w[:, :, c * 512:(c + 1) * 512]).then_inc(s, 16)
                pool.dma_start(w3[HID:HID + 1], b[:, :, c * 512:(c + 1) * 512]).then_inc(s, 16)

            load_w3(0, ld_w3)
            store_mods(3)
            load_bada(4)
            store_mods(4)
            load_bada(5)
            store_mods(5)
            pool.wait_ge(S["hy_done"], 12)
            pool.dma_start(window, consts["window"][:, :, 0:512]).then_inc(ld_w3, 16)
            pool.wait_ge(S["kab_done"], 3)
            load_w3(1, ld_w3b)
            pool.dma_start(window, consts["window"][:, :, 512:1024]).then_inc(ld_w3b, 16)
            pool.wait_ge(S["mrg_done"], 17)
            pool.dma_start(acc[:, 0, :], t["x_prompt"][0]).then_inc(ld_x2, 16)
            pool.dma_start(acc[:, 1:3, :], t["x_sample"][0].rearrange("(a p) n -> p a n", p=P)).then_inc(ld_x2, 16)
            for g in range(2):
                pool.dma_start(gate1[:, g, :], row(mods_dram[0, g], P)).then_inc(ld_g1, 16)
            pool.dma_start(ln1[:, 0, :], row(t["ln1_g"][0], P)).then_inc(ld_ln1, 16)
            pool.dma_start(ln1[:, 1, :], row(t["ln1_b"][0], P)).then_inc(ld_ln1, 16)
            pool.dma_start(w_router, t["w_router"][0].rearrange("(k p) n -> p k n", p=P)).then_inc(ld_wr, 16)
            through(pool, N_OUT + 7)
            for j in range(2):
                pool.dma_start(mod_s[:, j, :], row(mods_dram[1 + j, 1], P)).then_inc(ld_mods, 16)
            pool.wait_ge(S["wo_done"], 24)
            for j in range(2):
                pool.dma_start(mod_c[:, j, :], row(mods_dram[1 + j, 0], P)).then_inc(ld_modc, 16)
            pool.wait_ge(S["h2_done"], 3)
            for half in range(2):
                for j, g in enumerate((1, 0)):
                    p0 = 64 * half + 32 * j
                    src = mods_dram[3, g, half * 1024:(half + 1) * 1024]
                    pool.dma_start(g2[p0:p0 + 32].rearrange("p a b -> p (a b)"), row(src, 32)).then_inc(ld_g2, 16)
            pool.wait_ge(S["lg_ps"], 3)
            pool.dma_start(ln2[:, 0, :], row(t["ln2_g"][0], P)).then_inc(ld_ln2, 16)
            pool.dma_start(ln2[:, 1, :], row(t["ln2_b"][0], P)).then_inc(ld_ln2, 16)

        @block.tensor
        def _(pe):
            def arrive(n):
                pe.wait_ge(full[n % RING], filled[n])

            def release(mm, n):
                mm.then_inc(used[n % RING], 1)

            def ada(n):
                _, m, k = stream[n]
                arrive(n)
                if k == 0 and m >= 2:
                    pe.wait_ge(S["ada_rows"], m - 1)
                if k == 0 and m >= 3:
                    pe.wait_ge(S["pT_done"], H)
                    pe.wait_ge(S["av_done"], H)
                w = slot(n, 2, D)
                for j in range(2):
                    for g in range(4):
                        mm = pe.matmul(ps[6 + m % 2][32 * g:32 * g + 2, :], condT[:, :, 2 * k + j],
                                       w[:, j, g * 512:(g + 1) * 512],
                                       start=(k == 0 and j == 0), stop=(k == 7 and j == 1))
                release(mm, n)

            def rows_to_columns(m):
                pe.wait_ge(S["ada_rows"], m + 1)
                if m:
                    pe.wait_ge(S["col_done"], m)
                for b in range(4):
                    for g in range(4):
                        mm = pe.matmul(ps[2 + g][:, 2 * b:2 * b + 2], stage[32 * g:32 * g + 2, b * P:(b + 1) * P],
                                       ident[32 * g:32 * g + 2, 32 * g:32 * g + 2], start=True, stop=True)
                mm.then_inc(S["col_ps"], 1)

            def attention(n):
                w = slot(n, 2, D)
                pe.wait_ge(S["uq_done"], 12)
                pe.wait_ge(ld_att, 80)
                for p0 in range(4):
                    pe.matmul(ps[p0][:, 0:LS], perm, qR[:, p0, LC:NT], start=True, stop=True)\
                        .then_inc(S["rot_ps"], 1)
                pe.wait_ge(S["ada_rows"], 3)
                for kb in range(4):
                    for half in range(2):
                        pe.transpose(ps[4 + half][:, kb * P:(kb + 1) * P],
                                     ckv[:, kb, half * P:(half + 1) * P], ident)
                    mm = pe.transpose(ps[6][:, kb * P:(kb + 1) * P], kr[:, kb, :], ident)
                mm.then_inc(S["kvT_ps"], 1)
                pe.wait_ge(S["kvT_done"], 3)
                pe.wait_ge(S["rot_done"], 4)
                for kb in range(4):
                    for half in range(2):
                        m = 2 * kb + half
                        for k in range(2):
                            rhs = w[:, k, half * 1024:(half + 1) * 1024]\
                                .rearrange("p (h c) -> p h c", c=256)[:, :, NOPE:256]
                            mm = pe.matmul(ps[m][:, :].rearrange("p (h c) -> p h c", c=P),
                                           kvT[:, k, kb * P:(kb + 1) * P], rhs, start=(k == 0), stop=(k == 1))
                        mm.then_inc(S["val_ps"], 1)
                pe.wait_ge(S["val_done"], 8)

                def keys(h):
                    if h >= 1:
                        pe.wait_ge(S["kT_done"], h)
                    for k in range(2):
                        mm = pe.matmul(ps[0][:, :], w[:, k, h * 256:h * 256 + NOPE], kvT[:, k, :],
                                       start=(k == 0), stop=(k == 1))
                    if h == H - 1:
                        release(mm, n)
                    else:
                        mm.then_inc(S["kT_ps"], 1)

                def scores(h):
                    pe.wait_ge(S["kT_done"], h + 1)
                    if h >= 2:
                        pe.wait_ge(S["exp_done"], 3 * (h - 1))
                    r0 = 64 * (h % 2)
                    b0, b1 = ps[1 + 2 * (h % 2)], ps[2 + 2 * (h % 2)]
                    for tile, out, k0, k1 in ((0, b0[:, 0:P], 0, P), (1, b0[:, P:512], P, 512),
                                              (2, b1[:, 0:384], P, 512)):
                        tok = slice(tile * P, (tile + 1) * P)
                        pe.matmul(out, qN[:, h, tok], kT[:, h % 2, k0:k1], start=True, stop=False)
                        mm = pe.matmul(out, qR[r0:r0 + ROPE, h // 2, tok], krT[r0:r0 + ROPE, k0:k1],
                                       start=False, stop=True)
                    mm.then_inc(S["sc_ps"], 1)

                def turn(h):
                    pe.wait_ge(S["prob_done"], h + 1)
                    if h >= 1:
                        pe.wait_ge(S["pT_done"], h)
                    pr = prob[:, h % 2, :]
                    pe.transpose(ps[5][:, 0:P], pr[:, 0:P], ident)
                    for kb in range(3):
                        for tile in range(2):
                            out = (ps[5][:, P + tile * P:2 * P + tile * P] if kb == 0 else
                                   ps[6][:, (kb - 1) * LS + tile * P:(kb - 1) * LS + (tile + 1) * P])
                            c0 = P + tile * 384 + kb * P
                            mm = pe.transpose(out, pr[:, c0:c0 + P], ident)
                    mm.then_inc(S["pT_ps"], 1)

                def attend(h):
                    pe.wait_ge(S["pT_done"], h + 1)
                    if h >= 1:
                        pe.wait_ge(S["av_done"], h)
                    pT = probT[:, h % 2, :]
                    hc = slice(h * VH, (h + 1) * VH)
                    pe.matmul(ps[7][:, 0:LC], vals[:, 0, hc], pT[:, 0:P], start=True, stop=True)
                    for kb in range(3):
                        mm = pe.matmul(ps[7][:, LC:NT], vals[:, 1 + kb, hc],
                                       pT[:, P + kb * LS:P + (kb + 1) * LS], start=(kb == 0), stop=(kb == 2))
                    mm.then_inc(S["av_ps"], 1)

                keys(0)
                scores(0)
                keys(1)
                for h in range(H):
                    if h + 1 < H:
                        scores(h + 1)
                    if h + 2 < H:
                        keys(h + 2)
                    turn(h)
                    attend(h)

            def hyena():
                pe.wait_ge(S["hy_done"], 12)
                pe.wait_ge(ld_dft, 16)
                pe.wait_ge(S["ada_rows"], 6)
                pe.wait_ge(S["ones_done"], 1)
                kp = kn = kf = 0
                for c in range(2):
                    if c:
                        pe.wait_ge(S["hyT_done"], 4)
                        pe.wait_ge(S["pq_done"], 3)
                    for b in range(4):
                        for tile in range(3):
                            mm = pe.transpose(ps[tile][:, b * P:(b + 1) * P],
                                              zT[:, 4 * c + b, tile * P:(tile + 1) * P], ident)
                    mm.then_inc(S["zt_ps"], 1)
                    pe.wait_ge((ld_w3, ld_w3b)[c], 48)
                    for lat in (1, 0):
                        for i, pb in enumerate((1, 2) if lat else (0,)):
                            bf, bb = (ps[3 + 2 * i], ps[4 + 2 * i]) if lat else (ps[0], ps[1])
                            for d, bank in enumerate((bf, bb)):
                                mm = pe.matmul(bank[:, :], hdn[:, pb * P:(pb + 1) * P], w3[:, d, :],
                                               start=True, stop=True)
                            mm.then_inc(S["kp_ps"], 1)
                        for i in range(2 if lat else 1):
                            kp += 1
                            pe.wait_ge(S["kab_done"], kp)
                            for b in range(4):
                                mm = pe.matmul((ps[7] if lat else ps[2])[:, 4 * i + b:4 * i + b + 1],
                                               ktmp2[:, b * P:(b + 1) * P], ones, start=True, stop=True)
                            mm.then_inc(S["kn_ps"], 1)
                        nf = 2 if lat else 1
                        banks = [ps[3], ps[4], ps[5], ps[6]] if lat else [ps[7], ps[0]]
                        fwd = (lambda cs, pb, fb: f256[:, cs, pb, fb * P:(fb + 1) * P]) if lat else \
                              (lambda cs, pb, fb: f128[:, cs, :])
                        for cs, src in enumerate((kA, kB)):
                            for fb in range(nf):
                                bank = banks[cs * nf + fb]
                                for pb in range(nf):
                                    mm = pe.matmul(bank[:, :], fwd(cs, pb, fb), src[:, pb, :],
                                                   start=(pb == 0), stop=(pb == nf - 1))
                        mm.then_inc(S["kf_ps"], 1)
                        kn += 1
                        pe.wait_ge(S["kn_done"], kn)
                        pe.wait_ge(S["zt_done"], 3 * (c + 1))
                        banks = [ps[0], ps[1], ps[2], ps[7]] if lat else [ps[1], ps[2]]
                        for cs in range(2):
                            for fb in range(nf):
                                bank = banks[cs * nf + fb]
                                for pb in range(nf):
                                    mm = pe.matmul(bank[:, :], fwd(cs, pb, fb), z_tok[:, lat + pb, :],
                                                   start=(pb == 0), stop=(pb == nf - 1))
                        mm.then_inc(S["zf_ps"], 1)
                        pe.wait_ge(S["kf_done"], 2 * c + (1 if lat else 2))
                        pe.wait_ge(S["pq_done"], 3 * c + (2 if lat else 3))
                        for b in range(4):
                            out = ps[3 + b][:, LC:NT] if lat else ps[3 + b][:, 0:LC]
                            for cs, src in enumerate((spP, spQ)):
                                for fb in range(nf):
                                    inv = i256[:, cs, fb, :] if lat else i128[:, cs, :]
                                    mm = pe.matmul(out, src[:, fb, b * P:(b + 1) * P], inv,
                                                   start=(cs == 0 and fb == 0), stop=(cs == 1 and fb == nf - 1))
                            if lat == 0 or b == 3:
                                mm.then_inc(S["yT_ps"], 1)

            def gates():
                pe.wait_ge(S["hyT_done"], 8)
                pe.wait_ge(S["av_done"], H)
                with pe.Fori(0, 4) as i:
                    for sub in range(2):
                        n = N_PRE + 3 * sub
                        for j2, bank0 in ((0, 0), (1, 2)):
                            m = n + j2
                            s = m % RING
                            pe.wait_ge(full[s], i * per_turn[s] + filled[m])
                            pe.wait_ge(S[("sig_a", "sig_b")[j2]], i * 2 + sub + 1)
                            w = slot(m, KD, 256)
                            for j in range(2):
                                for k in range(KD):
                                    mm = pe.matmul(ps[bank0 + j][:, 0:NT], w[:, k, j * P:(j + 1) * P],
                                                   hT[:, k, :], start=(k == 0), stop=(k == KD - 1))
                            release(mm, m)
                        m = n + 2
                        s = m % RING
                        pe.wait_ge(full[s], i * per_turn[s] + filled[m])
                        pe.wait_ge(S["mrg_done"], i * 4 + 2 * sub + 1)
                        w = slot(m, 2, 8, 256)
                        for half, src in enumerate((attT, x0T)):
                            for j in range(2):
                                for k in range(8):
                                    mm = pe.matmul(ps[4 + 2 * half + j][:, 0:NT],
                                                   w[:, half, k, j * P:(j + 1) * P], src[:, k, :],
                                                   start=(k == 0), stop=(k == 7))
                        release(mm, m)

            def output_projection():
                pe.wait_ge(S["mrg_done"], 17)
                for j in range(8):
                    n = N_OUT + j
                    arrive(n)
                    if j >= 2:
                        pe.wait_ge(S["wo_done"], 3 * (j - 1))
                    w = slot(n, KD, 256)
                    for tile in range(3):
                        for k in range(KD):
                            mm = pe.matmul(ps[3 * (j % 2) + tile][:, 0:256],
                                           mergedT[:, k, tile * P:(tile + 1) * P], w[:, k, :],
                                           start=(k == 0), stop=(k == KD - 1))
                    release(mm, n)

            def routing():
                pe.wait_ge(S["wo_done"], 24)
                pe.wait_ge(ld_wr, 16)
                for tile in range(3):
                    pe.wait_ge(S["h2_done"], 3 if tile == 0 else tile + 1)
                    for q in range(4):
                        m = 4 * tile + q
                        if m >= 6:
                            pe.wait_ge(S["h2T_done"], m - 5)
                        for b in range(4):
                            kb = 4 * q + b
                            mm = pe.transpose(ps[m % 6][:, b * P:(b + 1) * P], h2[:, tile, kb * P:(kb + 1) * P], ident)
                        mm.then_inc(S["h2T_ps"], 1)
                for tile in range(3):
                    pe.wait_ge(S["h2T_done"], 4 * (tile + 1))
                    for k in range(KD):
                        mm = pe.matmul(ps[6][:, tile * NE:(tile + 1) * NE], h2T[:, k, tile * P:(tile + 1) * P],
                                       w_router[:, k, :], start=(k == 0), stop=(k == KD - 1))
                    mm.then_inc(S["lg_ps"], 1)
                pe.wait_ge(S["aff_done"], 1)
                for tile in range(3):
                    mm = pe.transpose(ps[7][0:NE, tile * P:(tile + 1) * P], aff[:, tile, :], ident)
                mm.then_inc(S["affT_ps"], 1)
                pe.wait_ge(S["affT_done"], 1)
                for e in range(NE):
                    if e >= 4:
                        pe.wait_ge(S["br_used"], e - 3)
                    pe.matmul(ps[e % 4][:, 0:NT], ident[0:NE, e:e + 1].to_broadcast([NE, P]), affT,
                              start=True, stop=True).then_inc(S["br_ps"], 1)

            def experts():
                pe.wait_ge(S["br_used"], NE)

                def gather():
                    for k in range(KD):
                        out = ps[6 + k // 8][:, (k % 8) * 64:(k % 8) * 64 + 48]
                        blk = slice(k * P, (k + 1) * P)
                        pe.matmul(out[:, 0:CAP_S], h2[:, 1, blk], pick[:, 1, :], start=True, stop=False)
                        pe.matmul(out[:, 0:CAP_S], h2[:, 2, blk], pick[:, 2, :], start=False, stop=True)
                        mm = pe.matmul(out[:, CAP_S:48], h2[:, 0, blk], pick[:, 0, 0:CAP_C], start=True, stop=True)
                    mm.then_inc(S["xe_ps"], 1)

                pe.wait_ge(S["pick_done"], 1)
                gather()
                with pe.Fori(0, NE) as e:
                    pe.wait_ge(S["xe_d"], e + 1)
                    pe.wait_ge(S["xe_a"], e + 1)
                    pe.wait_ge(S["cb_used"], e * 12 + 1)
                    for j in range(8):
                        n = N_EXP + j
                        s = n % RING
                        pe.wait_ge(full[s], e * 32 + exp_fill0[s] + 16 * (1 + j // RING))
                        w = slot(n, 4, FF)
                        for k4 in range(4):
                            k = 4 * (j % 4) + k4
                            for half in range(2):
                                mm = pe.matmul(ps[j // 4][64 * half:64 * half + 64, :], xe[:, k, :],
                                               w[:, k4, half * 512:(half + 1) * 512],
                                               start=(k == 0), stop=(k == KD - 1))
                        release(mm, n)
                    pe.wait_ge(S["give_done"], e + 1)
                    for tile in range(3):
                        mm = pe.transpose(ps[5][:, tile * P:(tile + 1) * P], give[:, tile, :], ident)
                    mm.then_inc(S["comb_ps"], 1)
                    pe.wait_ge(S["pick_done"], e + 2)
                    gather()
                    pe.wait_ge(S["hid_done"], e + 1)
                    for b in range(4):
                        mm = pe.transpose(ps[2][:, b * P:(b + 1) * P], hid[:, b * P:(b + 1) * P], ident)
                    mm.then_inc(S["hT_ps"], 1)
                    pe.wait_ge(S["hT_done"], e + 1)
                    for j in range(8, 12):
                        n = N_EXP + j
                        s = n % RING
                        pe.wait_ge(full[s], e * 32 + exp_fill0[s] + 16 * (1 + j // RING))
                        w = slot(n, 2, D)
                        for k2 in range(2):
                            k = 2 * (j - 8) + k2
                            for u in (0, 2, 1, 3):
                                half = u // 2
                                mm = pe.matmul(ps[3 + u % 2][64 * half:64 * half + 64, :],
                                               hidT[:, k % 4, 64 * (k // 4):64 * (k // 4) + 64],
                                               w[:, k2, u * 512:(u + 1) * 512],
                                               start=(k == 0), stop=(k == 7))
                        release(mm, n)
                    pe.wait_ge(S["comb_done"], e + 1)
                    pe.wait_ge(S["xe_d"], e + 2)
                    pe.wait_ge(S["xe_a"], e + 2)
                    pe.wait_ge(S["ye_done"], e + 1)
                    for q in range(12):
                        tile, u = q // 4, (0, 2, 1, 3)[q % 4]
                        r0 = 64 * (u // 2)
                        if q >= 6:
                            pe.wait_ge(S["cb_used"], e * 12 + q - 4)
                        pe.matmul(ps[SCATTER_BANKS[q % 6]][:, :], comb[r0:r0 + 64, tile, :],
                                  ye[r0:r0 + 64, u % 2, :], start=True, stop=True).then_inc(S["cb_ps"], 1)

            pe.wait_ge(ld_const, 16)
            pe.wait_ge(S["silu_done"], 1)
            pe.transpose(ps[0][:, 0:32], c_rows, ident[0:32, 0:32]).then_inc(S["condT_ps"], 1)
            pe.wait_ge(ld_vec, 64)
            pe.transpose(ps[1][:, 0:108], vec_rows, ident[0:108, 0:108]).then_inc(S["vec_ps"], 1)
            pe.wait_ge(ld_x, 32)
            for b in range(KD):
                if b >= 4:
                    pe.wait_ge(S["xT_done"], b - 3)
                for tile in range(3):
                    mm = pe.transpose(ps[2 + b % 4][:, tile * P:(tile + 1) * P],
                                      acc[:, tile, b * P:(b + 1) * P], ident)
                mm.then_inc(S["xT_ps"], 1)
            pe.wait_ge(ld_filt, 112)
            pe.wait_ge(S["condT_done"], 1)
            pe.matmul(ps[0][0:HID, 0:NT], fw1, feats, start=True, stop=True).then_inc(S["filt_ps"], 1)
            for n in range(8):
                ada(n)
            pe.wait_ge(S["sin_done"], 1)
            pe.wait_ge(S["vec_done"], 1)
            pe.matmul(ps[1][0:HID, 0:NT], fw2, fh1, start=True, stop=True).then_inc(S["filt_ps"], 1)
            for n in range(8, 16):
                ada(n)
                if n == 9:
                    pe.wait_ge(S["xT_done"], KD)
                    rows_to_columns(0)
            rows_to_columns(1)

            tile_bank = (4, 5, 0)
            hy_n = 0
            for n in range(16, N_PRE):
                kind, a, b = stream[n]
                if kind == "ada":
                    ada(n)
                    continue
                arrive(n)
                if kind == "q":
                    w = slot(n, KD, 256)
                    if a == 0:
                        pe.wait_ge(S["farg_done"], 2)
                        pe.wait_ge(S["col_done"], 2)
                    for k in range(KD):
                        if a == 0:
                            pe.wait_ge(S["mod_lat"], k + 1)
                            pe.wait_ge(S["mod_ctx"], k + 1)
                        for j in range(2):
                            mm = pe.matmul(ps[2 * a + j][:, 0:NT], w[:, k, j * P:(j + 1) * P], hT[:, k, :],
                                           start=(k == 0), stop=(k == KD - 1))
                    release(mm, n)
                elif kind == "kv":
                    w = slot(n, KD, KVL)
                    pe.wait_ge(S["q_done"], 2)
                    pe.wait_ge(S["qsq_done"], 2)
                    for tile in range(3):
                        for k in range(KD):
                            mm = pe.matmul(ps[tile_bank[tile]][:, 0:KVL], hT[:, k, tile * P:(tile + 1) * P],
                                           w[:, k, :], start=(k == 0), stop=(k == KD - 1))
                    release(mm, n)
                elif kind == "kr":
                    w = slot(n, KD, ROPE)
                    for tile in range(3):
                        for k in range(KD):
                            mm = pe.matmul(ps[tile_bank[tile]][:, KVL:KVL + ROPE],
                                           hT[:, k, tile * P:(tile + 1) * P],
                                           w[:, k, :], start=(k == 0), stop=(k == KD - 1))
                    release(mm, n)
                    pe.wait_ge(S["q_done"], 4)
                    pe.wait_ge(S["qsq_done"], 4)
                    for tile in range(3):
                        for k in range(4):
                            mm = pe.matmul(ps[1][:, tile:tile + 1], qsq[:, k, tile * P:(tile + 1) * P], ones,
                                           start=(k == 0), stop=(k == 3))
                    mm.then_inc(S["qsum_ps"], 1)
                elif kind == "uq":
                    w = slot(n, 4, 768)
                    if a == 0:
                        pe.wait_ge(S["kv_tok"], 3)
                        pe.wait_ge(S["rq_done"], 1)
                    for j in range(6):
                        m = 6 * a + j
                        if m >= 6:
                            pe.wait_ge(S["uq_done"], m - 5)
                        for k in range(4):
                            if j < 4:
                                mm = pe.matmul(ps[j][:, 0:NT], w[:, k, j * 192:j * 192 + NOPE], qc[:, k, :],
                                               start=(k == 0), stop=(k == 3))
                                continue
                            for r in range(2):
                                c0 = (2 * (j - 4) + r) * 192 + NOPE
                                mm = pe.matmul(ps[j][64 * r:64 * r + 64, 0:NT], w[:, k, c0:c0 + ROPE], qc[:, k, :],
                                               start=(k == 0), stop=(k == 3))
                        if j < 5:
                            mm.then_inc(S["uq_ps"], 1)
                    release(mm, n)
                elif kind == "ukv":
                    attention(n)
                else:
                    if hy_n == 0:
                        pe.wait_ge(S["kT_done"], H)
                        pe.wait_ge(S["exp_done"], 3 * H)
                        pe.wait_ge(S["pT_done"], H)
                    if hy_n >= 3:
                        pe.wait_ge(S["hy_done"], hy_n - 2)
                    w = slot(n, KD, 256)
                    for j in range(2):
                        for k in range(KD):
                            mm = pe.matmul(ps[2 * (hy_n % 3) + j][:, 0:NT], w[:, k, j * P:(j + 1) * P],
                                           hT[:, k, :], start=(k == 0), stop=(k == KD - 1))
                    release(mm, n)
                    hy_n += 1

            hyena()
            gates()
            output_projection()
            routing()
            experts()

        @block.scalar
        def _(act):
            ch = Chain(act, av)
            act.dma_start(acc[:, 0, :], t["x_prompt"][0]).then_inc(ld_x, 16)
            act.dma_start(acc[:, 1:3, :], t["x_sample"][0].rearrange("(a p) n -> p a n", p=P)).then_inc(ld_x, 16)
            act.wait_ge(ld_c, 32)
            act.activation(c_rows, c_rows, ACT.Silu).then_inc(S["silu_done"], 1)
            act.wait_ge(S["farg_done"], 1)
            act.activation(fh1, farg, ACT.Sin).then_inc(S["sin_done"], 1)
            act.wait_ge(S["farg_done"], 2)
            act.activation(hdn[0:HID, :], farg, ACT.Sin).then_inc(S["sin_done"], 1)
            act.wait_ge(S["col_done"], 2)
            for b in range(KD):
                act.activation(hT[:, b, 0:LC], hT[:, b, 0:LC], ACT.Identity, bias=modc[:, 0, 0, b:b + 1],
                               scale=modc[:, 1, 0, b:b + 1]).then_inc(S["mod_ctx"], 1)
            for a in range(2):
                for j in range(2):
                    act.wait_ge(S["q_done"], 2 * a + j + 1)
                    act.activation(qsq[:, 2 * a + j, :], ps[2 * a + j][:, 0:NT], ACT.Square)\
                       .then_inc(S["qsq_done"], 1)
            through(act, stream.index(("kr", 0, 0)))
            for tile, bank in enumerate((4, 5, 0)):
                ch.link(act.activation(kv_junk, ps[bank][:, 0:KVL], ACT.Square, accum_out=ss_kv[:, tile:tile + 1]))
            act.activation(kv_junk[:, 0:1], ss_kv[:, 0:1], ACT.Copy).then_inc(S["kv_sq"], 1)
            act.wait_ge(S["kv_var"], 1)
            act.activation(r_kv, r_kv, ACT.Sqrt).then_inc(S["kv_std"], 1)
            act.wait_ge(S["q_var"], 1)
            act.activation(rq, rq, ACT.Sqrt).then_inc(S["q_std"], 1)
            for a in range(2):
                n = stream.index(("uq", a, 0))
                for j in range(6):
                    if j < 5:
                        act.wait_ge(S["uq_ps"], 5 * a + j + 1)
                    else:
                        through(act, n)
                    dst = qN[:, 4 * a + j, :] if j < 4 else qR[:, 2 * a + j - 4, :]
                    act.activation(dst, ps[j][:, 0:NT], ACT.Copy).then_inc(S["uq_done"], 1)
            act.wait_ge(S["kvT_ps"], 1)
            for half in range(2):
                act.activation(kvT[:, half, :], ps[4 + half][:, :], ACT.Copy).then_inc(S["kvT_done"], 1)
            act.activation(krT, ps[6][:, :], ACT.Copy).then_inc(S["kvT_done"], 1)
            for m in range(8):
                act.wait_ge(S["val_ps"], m + 1)
                act.activation(vals[:, m // 2, (m % 2) * 512:(m % 2 + 1) * 512], ps[m][:, :], ACT.Copy)\
                   .then_inc(S["val_done"], 1)

            def keys_copy(h):
                if h == H - 1:
                    through(act, stream.index(("ukv", 0, 0)))
                else:
                    act.wait_ge(S["kT_ps"], h + 1)
                if h >= 2:
                    act.wait_ge(S["sc_ps"], h - 1)
                act.activation(kT[:, h % 2, :], ps[0][:, :], ACT.Copy).then_inc(S["kT_done"], 1)

            def exps(h):
                act.wait_ge(S["nb_done"], h + 1)
                if h >= 2:
                    act.wait_ge(S["pT_ps"], h - 1)
                b0, b1 = ps[1 + 2 * (h % 2)], ps[2 + 2 * (h % 2)]
                for tile, src, c0, c1 in ((0, b0[:, 0:P], 0, P), (1, b0[:, P:512], P, 512), (2, b1[:, 0:384], 512, 896)):
                    act.activation(prob[:, h % 2, c0:c1], src, ACT.Exp, bias=snb[:, h % 2, tile:tile + 1],
                                   scale=rq[:, tile:tile + 1], accum_out=srs[:, h % 2, tile:tile + 1])\
                       .then_inc(S["exp_done"], 1)

            keys_copy(0)
            keys_copy(1)
            exps(0)
            for h in range(H):
                if h + 2 < H:
                    keys_copy(h + 2)
                if h + 1 < H:
                    exps(h + 1)
                act.wait_ge(S["av_ps"], h + 1)
                act.activation(attT[:, h, :], ps[7][:, 0:NT], ACT.Copy).then_inc(S["av_done"], 1)
            hy_n = 0
            for n in range(16, N_PRE):
                kind, part, c = stream[n]
                if kind != "hy":
                    continue
                through(act, n)
                if part == 1 and c:
                    act.wait_ge(S["hy_done"], 3 * c - 1)
                for j in range(2):
                    blk = 8 * part + 2 * c + j
                    dst = (x0T, None, zT)[part][:, 2 * c + j, :] if part != 1 else x1T[:, j, :]
                    act.activation(dst, ps[2 * (hy_n % 3) + j][:, 0:NT], ACT.Identity,
                                   bias=sb_[:, blk:blk + 1], scale=sw[:, 1, blk:blk + 1]).then_inc(S["hy_mid"], 1)
                hy_n += 1
            k = 0
            for c in range(2):
                for lat in (1, 0):
                    k += 1
                    act.wait_ge(S["kf_ps"], k)
                    if k > 1:
                        act.wait_ge(S["pq_done"], (2, 3, 5)[k - 2])
                    banks = [ps[3], ps[4], ps[5], ps[6]] if lat else [ps[7], ps[0]]
                    nf = 2 if lat else 1
                    for fb in range(nf):
                        act.activation(kSr[:, fb, :], banks[fb][:, :], ACT.Copy)
                        ins = act.activation(kSs[:, fb, :], banks[nf + fb][:, :], ACT.Copy)
                    ins.then_inc(S["kf_done"], 1)
            act.sem_inc(S["sig_a"], 1)
            act.sem_inc(S["sig_b"], 1)
            with act.Fori(0, 4) as i:
                for sub in range(2):
                    for g in range(2):
                        m = N_PRE + 3 * sub + g
                        act.wait_ge(used[m % RING], m // RING + 1 + i)
                        if g == 0:
                            act.wait_ge(S["mrg_done"], i * 4 + 2 * sub + 1)
                        for j in range(2):
                            ins = act.activation(sig[:, g, j, :], ps[2 * g + j][:, 0:NT], ACT.Sigmoid)
                        ins.then_inc(S[("sig_a", "sig_b")[g]], 1)
            for tile in range(3):
                act.wait_ge(S["var_done"], tile + 1)
                act.activation(rstd, rstd, ACT.Sqrt).then_inc(S["std_done"], 1)
                act.wait_ge(S["h2_done"], tile + 1)
                act.activation(acc[:, tile, :], acc[:, tile, :], ACT.Copy, scale=ALPHA).then_inc(S["x1_done"], 1)
            for tile in range(3):
                act.wait_ge(S["lmx_done"], tile + 1)
                act.activation(aff[:, tile, :], logits[:, tile * NE:(tile + 1) * NE], ACT.Exp,
                               bias=lsm[:, tile, 1:2], accum_out=lsm[:, tile, 2:3]).then_inc(S["lexp_done"], 1)

            def xe_copy(n):
                act.wait_ge(S["xe_ps"], n)
                act.activation(xe[:, 8:16, 0:48], ps[7][:, :].rearrange("p (k c) -> p k c", c=64)[:, :, 0:48],
                               ACT.Copy).then_inc(S["xe_a"], 1)

            xe_copy(1)
            with act.Fori(0, NE) as e:
                m = N_EXP + 3
                act.wait_ge(used[m % RING], m // RING + 1 + e * 2)
                act.activation(sil, ps[0][:, :], ACT.Silu).then_inc(S["sil_done"], 1)
                xe_copy(e + 2)
            for tile in range(3):
                act.wait_ge(S["var_done"], 4 + tile)
                act.activation(rstd, rstd, ACT.Sqrt).then_inc(S["std_done"], 1)

        @block.vector
        def _(dve):
            ch = Chain(dve, dv)
            link = ch.link

            dve.wait_ge(S["condT_ps"], 1)
            dve.tensor_copy(condT.rearrange("p a b -> p (a b)"), ps[0][:, 0:32]).then_inc(S["condT_done"], 1)
            dve.wait_ge(S["vec_ps"], 1)
            dve.tensor_copy(cols, ps[1][:, 0:108]).then_inc(S["vec_done"], 1)
            for b in range(KD):
                dve.wait_ge(S["xT_ps"], b + 1)
                dve.tensor_copy(hT[:, b, :], ps[2 + b % 4][:, 0:NT]).then_inc(S["xT_done"], 1)

            def filter_layer(n, bank):
                dve.wait_ge(S["filt_ps"], n + 1)
                dve.wait_ge(ld_filt, 112)
                if n:
                    dve.wait_ge(S["sin_done"], n)
                link(dve.tensor_scalar(farg, ps[bank][0:HID, 0:NT], fcol[0:HID, 2 * n:2 * n + 1],
                                       fcol[0:HID, 2 * n + 1:2 * n + 2], ALU.add, ALU.mult))
                link(dve.tensor_scalar(frnd, farg, 1.0 / (2.0 * math.pi), ROUND, ALU.mult, ALU.add))
                link(dve.tensor_scalar(frnd, frnd, ROUND, None, ALU.subtract))
                for part in (TWO_PI_HI, TWO_PI_MID, TWO_PI_LO):
                    link(dve.scalar_tensor_tensor(farg, frnd, -part, farg, ALU.mult, ALU.add))
                dve.tensor_scalar(farg, farg, 3.1415925, -3.1415925, ALU.min, ALU.max).then_inc(S["farg_done"], 1)

            def ada_rows(m):
                through(dve, stream.index(("ada", m, 7)))
                dve.wait_ge(ld_bada, 64 * (m + 1))
                for g in range(4):
                    rows = stage[32 * g:32 * g + 2, :]
                    ins = dve.scalar_tensor_tensor(rows, ps[6 + m % 2][32 * g:32 * g + 2, :],
                                                   1.0 if m in (1, 4) else 0.0, rows, ALU.add, ALU.add)
                ins.then_inc(S["ada_rows"], 1)

            def mod_columns(m):
                dve.wait_ge(S["col_ps"], m + 1)
                for g in range(4):
                    ins = dve.tensor_copy(modc[:, m, :, 4 * g:4 * g + 4],
                                          ps[2 + g][:, 0:8].rearrange("p (b c) -> p c b", c=2))
                ch.inc(ins)
                ch.wait()
                dve.sem_inc(S["col_done"], 1)

            filter_layer(0, 0)
            ada_rows(0)
            filter_layer(1, 1)
            mod_columns(0)
            ada_rows(1)
            mod_columns(1)
            for b in range(KD):
                dve.tensor_scalar(hT[:, b, LC:NT], hT[:, b, LC:NT], modc[:, 1, 1, b:b + 1], modc[:, 0, 1, b:b + 1],
                                  ALU.mult, ALU.add).then_inc(S["mod_lat"], 1)

            for a in range(2):
                through(dve, stream.index(("q", a, 0)))
                for j in range(2):
                    blk = 2 * a + j
                    dve.tensor_scalar(qc[:, blk, :], ps[blk][:, 0:NT], q_g[:, blk:blk + 1], None, ALU.mult)\
                       .then_inc(S["q_done"], 1)

            dve.wait_ge(S["kv_sq"], 1)
            dve.wait_ge(av, 3)
            dve.tensor_scalar(r_kv, ss_kv, 1.0 / KVL, EPS, ALU.mult, ALU.add).then_inc(S["kv_var"], 1)
            dve.wait_ge(S["kv_std"], 1)
            link(dve.reciprocal(r_kv, r_kv))
            dve.wait_ge(ld_att, 80)
            for tile, (bank, kb) in enumerate(((4, 0), (5, 2), (0, 3))):
                link(dve.scalar_tensor_tensor(ckv[:, kb, :], ps[bank][:, 0:KVL], r_kv[:, tile:tile + 1], kv_g,
                                              ALU.mult, ALU.mult))
                src = ps[bank][:, KVL:KVL + ROPE]
                dst = kr[:, kb, 0:ROPE]
                if tile == 0:
                    link(dve.tensor_copy(dst, src))
                else:
                    s3 = src.rearrange("p (x s f) -> p x s f", s=2, f=16)
                    d3 = dst.rearrange("p (x s f) -> p x s f", s=2, f=16)
                    cos = rope_k[:, 0, tile - 1, :].rearrange("p (x f) -> p x f", f=16)
                    sin = rope_k[:, 1, tile - 1, :].rearrange("p (x f) -> p x f", f=16)
                    t0 = ktmp[:, 0, :].rearrange("p (x f) -> p x f", f=16)
                    t1 = ktmp[:, 1, :].rearrange("p (x f) -> p x f", f=16)
                    for out_s, a_s, b_s, op in ((0, 0, 1, ALU.subtract), (1, 1, 0, ALU.add)):
                        ch.inc(dve.tensor_tensor(t0, s3[:, :, a_s, :], cos, ALU.mult))
                        link(dve.tensor_tensor(t1, s3[:, :, b_s, :], sin, ALU.mult))
                        link(dve.tensor_tensor(d3[:, :, out_s, :], t0, t1, op))
                dve.tensor_copy(kr[:, kb, ROPE:2 * ROPE], dst).then_inc(S["kv_tok"], 1)
            dve.wait_ge(S["qsum_ps"], 1)
            dve.tensor_scalar(rq, ps[1][:, 0:3], 1.0 / QL, EPS, ALU.mult, ALU.add).then_inc(S["q_var"], 1)
            dve.wait_ge(S["q_std"], 1)
            link(dve.reciprocal(rq, rq))
            link(dve.tensor_scalar(rq, rq, SCALE, None, ALU.mult))
            dve.sem_inc(S["rq_done"], 1)
            ada_rows(2)

            for p0 in range(4):
                dve.wait_ge(S["rot_ps"], p0 + 1)
                q = qR[:, p0, LC:NT]
                ch.inc(dve.tensor_tensor(rtmp, ps[p0][:, 0:LS], rope_q[:, 1, :], ALU.mult))
                link(dve.tensor_tensor(q, q, rope_q[:, 0, :], ALU.mult))
                link(dve.tensor_tensor(q, q, rtmp, ALU.add))
                dve.sem_inc(S["rot_done"], 1)

            def maxima(h):
                dve.wait_ge(S["sc_ps"], h + 1)
                b0, b1 = ps[1 + 2 * (h % 2)], ps[2 + 2 * (h % 2)]
                for tile, src in ((0, b0[:, 0:P]), (1, b0[:, P:512]), (2, b1[:, 0:384])):
                    ins = dve.tensor_reduce(smx[:, h % 2, tile:tile + 1], src, AX_X, ALU.max)
                link(ins)
                dve.scalar_tensor_tensor(snb[:, h % 2, :], smx[:, h % 2, :], -1.0, rq, ALU.mult, ALU.mult)\
                   .then_inc(S["nb_done"], 1)

            maxima(0)
            for h in range(H):
                if h + 1 < H:
                    maxima(h + 1)
                dve.wait_ge(S["exp_done"], 3 * (h + 1))
                link(dve.reciprocal(srr[:, h % 2, :], srs[:, h % 2, :]))
                for tile, c0, c1 in ((0, 0, P), (1, P, 512), (2, 512, 896)):
                    pr = prob[:, h % 2, c0:c1]
                    ins = dve.tensor_scalar(pr, pr, srr[:, h % 2, tile:tile + 1], None, ALU.mult)
                ins.then_inc(S["prob_done"], 1)
                dve.wait_ge(S["pT_ps"], h + 1)
                if h >= 2:
                    dve.wait_ge(S["av_ps"], h - 1)
                dve.tensor_copy(probT[:, h % 2, 0:384], ps[5][:, 0:384])
                dve.tensor_copy(probT[:, h % 2, 384:896], ps[6][:, :]).then_inc(S["pT_done"], 1)

            hy_n = 0
            for n in range(16, N_PRE):
                kind, part, c = stream[n]
                if kind != "hy":
                    continue
                for j in range(2):
                    dve.wait_ge(S["hy_mid"], 2 * hy_n + j + 1)
                    blk = 8 * part + 2 * c + j
                    dst = (x0T, None, zT)[part][:, 2 * c + j, :] if part != 1 else x1T[:, j, :]
                    src = ps[2 * (hy_n % 3) + j]
                    for g, a, b in GROUPS:
                        ins = dve.scalar_tensor_tensor(dst[:, a + 1:b], src[:, a:b - 1], sw[:, 0, blk:blk + 1],
                                                       dst[:, a + 1:b], ALU.mult, ALU.add)
                    link(ins)
                    for g, a, b in GROUPS:
                        ins = dve.scalar_tensor_tensor(dst[:, a:b - 1], src[:, a + 1:b], sw[:, 2, blk:blk + 1],
                                                       dst[:, a:b - 1], ALU.mult, ALU.add)
                    link(ins)
                    if part == 2:
                        link(dve.tensor_tensor(dst, dst, x1T[:, j, :], ALU.mult))
                dve.sem_inc(S["hy_done"], 1)
                hy_n += 1
                if hy_n % 4 == 0:
                    ada_rows(2 + hy_n // 4)

            kp = kn = zf = 0
            for c in range(2):
                dve.wait_ge(S["zt_ps"], c + 1)
                for tile in range(3):
                    dve.tensor_copy(z_tok[:, tile, :], ps[tile][:, :]).then_inc(S["zt_done"], 1)
                dve.wait_ge((ld_w3, ld_w3b)[c], 48)
                for lat in (1, 0):
                    if not lat:
                        dve.wait_ge(S["yT_ps"], 5 * c + 1)
                    elif c:
                        dve.wait_ge(S["yT_ps"], 5)
                    for i, pb in enumerate((1, 2) if lat else (0,)):
                        kp += 1
                        dve.wait_ge(S["kp_ps"], kp)
                        if kp > 1:
                            dve.wait_ge(S["kn_ps"], kp - 1)
                        bf, bb = (ps[3 + 2 * i], ps[4 + 2 * i]) if lat else (ps[0], ps[1])
                        ch.inc(dve.tensor_tensor(kA[:, i, :], bf[:, :], window[:, pb, :], ALU.mult))
                        if pb == 2:
                            link(dve.tensor_tensor(kB[:, i, :], bb[:, :], window[:, pb, :], ALU.mult))
                        else:
                            link(dve.scalar_tensor_tensor(kB[:, i, :], bb[:, :], bmask, window[:, pb, :],
                                                          ALU.mult, ALU.mult))
                        ch.inc(dve.scalar_tensor_tensor(ktmp2, kB[:, i, :], -1.0, kB[:, i, :], ALU.mult, ALU.max))
                        link(dve.scalar_tensor_tensor(bf[:, :], kA[:, i, :], -1.0, kA[:, i, :], ALU.mult, ALU.max))
                        link(dve.tensor_tensor(ktmp2, bf[:, :], ktmp2, ALU.add))
                        link(dve.tensor_tensor(kA[:, i, :], kA[:, i, :], kB[:, i, :], ALU.add))
                        dve.scalar_tensor_tensor(kB[:, i, :], kB[:, i, :], -2.0, kA[:, i, :], ALU.mult, ALU.add)\
                           .then_inc(S["kab_done"], 1)
                    dve.wait_ge(S["kn_ps"], kp)
                    rn = rnorm[:, lat, 4 * c:4 * c + 4]
                    if lat:
                        link(dve.tensor_copy(nsum[:, 0:4], ps[7][:, 0:4]))
                        link(dve.scalar_tensor_tensor(rn, ps[7][:, 4:8], EPS, nsum[:, 0:4], ALU.add, ALU.add))
                    else:
                        link(dve.tensor_scalar(rn, ps[2][:, 0:4], EPS, None, ALU.add))
                    dve.reciprocal(rn, rn).then_inc(S["kn_done"], 1)
                    zf += 1
                    dve.wait_ge(S["zf_ps"], zf)
                    dve.wait_ge(S["kf_done"], zf)
                    nf = 2 if lat else 1
                    banks = [ps[0], ps[1], ps[2], ps[7]] if lat else [ps[1], ps[2]]
                    for fb in range(nf):
                        zr, zs = banks[fb][:, :], banks[nf + fb][:, :]
                        if fb:
                            dve.wait_ge(S["pq_done"], pq)
                        ch.inc(dve.tensor_tensor(spP[:, fb, :], zr, kSr[:, fb, :], ALU.mult))
                        link(dve.tensor_tensor(ktmp2, zs, kSs[:, fb, :], ALU.mult))
                        link(dve.tensor_tensor(spP[:, fb, :], spP[:, fb, :], ktmp2, ALU.subtract))
                        ch.inc(dve.tensor_tensor(spQ[:, fb, :], zr, kSs[:, fb, :], ALU.mult))
                        link(dve.tensor_tensor(ktmp2, zs, kSr[:, fb, :], ALU.mult))
                        dve.tensor_tensor(spQ[:, fb, :], spQ[:, fb, :], ktmp2, ALU.add).then_inc(S["pq_done"], 1)
                        pq = 3 * c + (1 + fb if lat else 3)
                yt = ktmp2[:, 0:NT]
                for b in range(4):
                    dve.wait_ge(S["yT_ps"], 5 * c + 2 + b)
                    blk = 4 * c + b
                    for g, a0, b0 in GROUPS:
                        ins = dve.tensor_scalar(yt[:, a0:b0], ps[3 + b][:, a0:b0], rnorm[:, g, blk:blk + 1], None,
                                                ALU.mult)
                    link(ins)
                    link(dve.scalar_tensor_tensor(yt, zT[:, blk, :], skip[:, blk:blk + 1], yt, ALU.mult, ALU.add))
                    link(dve.tensor_tensor(x0T[:, blk, :], x0T[:, blk, :], yt, ALU.mult))
                    dve.sem_inc(S["hyT_done"], 1)

            dve.sem_inc(S["mrg_done"], 1)
            per = 6
            ch.base, ch.n = ch.base + ch.n, 0
            base = ch.base
            with dve.Fori(0, 4) as i:
                ch.base = i * per + base
                for sub in range(2):
                    m = N_PRE + 3 * sub + 2
                    dve.wait_ge(used[m % RING], m // RING + 1 + i)
                    dve.wait_ge(S["sig_a"], i * 2 + sub + 2)
                    dve.wait_ge(S["sig_b"], i * 2 + sub + 2)
                    for j in range(2):
                        ch.inc(dve.tensor_tensor(gsum[:, j, :], ps[4 + j][:, 0:NT], sig[:, 0, j, :], ALU.mult))
                        link_ = dve.tensor_tensor(sig[:, 1, j, :], ps[6 + j][:, 0:NT], sig[:, 1, j, :], ALU.mult)
                    link(link_)
                    for j in range(2):
                        dst = mergedT[:, bass.ds(i * 4 + 2 * sub + j, 1), :].rearrange("p a b -> p (a b)")
                        dve.tensor_tensor(dst, gsum[:, j, :], sig[:, 1, j, :], ALU.add).then_inc(S["mrg_done"], 1)
                assert ch.n == 6
            ch.base, ch.n = base + 4 * per, 0

            for j in range(8):
                through(dve, N_OUT + j)
                if j == 0:
                    dve.wait_ge(ld_x2, 32)
                    dve.wait_ge(ld_g1, 32)
                for tile in range(3):
                    cs = slice(j * 256, (j + 1) * 256)
                    tmp = wtmp[:, tile, :]
                    link(dve.tensor_tensor(tmp, ps[3 * (j % 2) + tile][:, 0:256], gate1[:, min(tile, 1), cs], ALU.mult))
                    dve.scalar_tensor_tensor(acc[:, tile, cs], acc[:, tile, cs], ALPHA, tmp, ALU.mult, ALU.add)\
                       .then_inc(S["wo_done"], 1)

            def normalise(tile, n):
                for q in range(4):
                    ins = dve.bn_stats(stat[:, 6 * q:6 * q + 6], acc[:, tile, q * 512:(q + 1) * 512])
                link(ins)
                link(dve.bn_aggr(mv, stat))
                dve.tensor_scalar(rstd[:, 0:1], mv[:, 1:2], EPS, None, ALU.add).then_inc(S["var_done"], 1)
                dve.wait_ge(S["std_done"], n)
                link(dve.reciprocal(rstd[:, 0:1], rstd[:, 0:1]))
                link(dve.tensor_scalar(acc[:, tile, :], acc[:, tile, :], mv[:, 0:1], rstd[:, 0:1],
                                       ALU.subtract, ALU.mult))

            dve.wait_ge(S["wo_done"], 24)
            link(dve.memset(rstd, 1.0))
            dve.wait_ge(ld_ln1, 32)
            for tile in range(3):
                normalise(tile, tile + 1)
                link(dve.tensor_tensor(acc[:, tile, :], acc[:, tile, :], ln1[:, 0, :], ALU.mult))
                link(dve.tensor_tensor(acc[:, tile, :], acc[:, tile, :], ln1[:, 1, :], ALU.add))
                mods, ready = (mod_c, ld_modc) if tile == 0 else (mod_s, ld_mods)
                dve.wait_ge(ready, 32)
                link(dve.tensor_tensor(h2[:, tile, :], acc[:, tile, :], mods[:, 1, :], ALU.mult))
                dve.tensor_tensor(h2[:, tile, :], h2[:, tile, :], mods[:, 0, :], ALU.add).then_inc(S["h2_done"], 1)

            dve.wait_ge(S["h2_done"], 3)
            for m in range(12):
                dve.wait_ge(S["h2T_ps"], m + 1)
                tile, q = m // 4, m % 4
                dve.tensor_copy(h2T[:, 4 * q:4 * q + 4, tile * P:(tile + 1) * P],
                                ps[m % 6][:, :].rearrange("p (b c) -> p b c", c=P)).then_inc(S["h2T_done"], 1)
            dve.wait_ge(S["lg_ps"], 3)
            link(dve.tensor_copy(logits, ps[6][:, 0:3 * NE]))
            for tile in range(3):
                link(dve.tensor_reduce(lsm[:, tile, 0:1], logits[:, tile * NE:(tile + 1) * NE], AX_X, ALU.max))
                dve.tensor_scalar(lsm[:, tile, 1:2], lsm[:, tile, 0:1], -1.0, None, ALU.mult)\
                   .then_inc(S["lmx_done"], 1)
            for tile in range(3):
                dve.wait_ge(S["lexp_done"], tile + 1)
                link(dve.reciprocal(lsm[:, tile, 3:4], lsm[:, tile, 2:3]))
                link(dve.tensor_scalar(aff[:, tile, :], aff[:, tile, :], lsm[:, tile, 3:4], None, ALU.mult))
            dve.sem_inc(S["aff_done"], 1)
            dve.wait_ge(S["affT_ps"], 1)
            dve.tensor_copy(affT, ps[7][0:NE, 0:NT]).then_inc(S["affT_done"], 1)

            for e in range(NE):
                dve.wait_ge(S["br_ps"], e + 1)
                row = ps[e % 4]
                for c, (tile, a, b, op) in enumerate(((0, 0, LC, ALU.is_gt), (0, 0, LC, None),
                                                      (1, LC, NT, ALU.is_gt), (1, LC, 2 * LC, None),
                                                      (2, LC, 2 * LC, ALU.is_ge), (2, 2 * LC, NT, ALU.is_gt),
                                                      (2, 2 * LC, NT, None))):
                    mine = aff[:, tile, e:e + 1]
                    if op is None:
                        ins = dve.scalar_tensor_tensor(junk[:, 0:P], row[:, a:b], mine, tri, ALU.is_equal, ALU.mult,
                                                       accum_out=cnt[:, c, e:e + 1])
                    else:
                        ins = dve.tensor_scalar(junk[:, 0:b - a], row[:, a:b], mine, None, op, ALU.add,
                                                accum_out=cnt[:, c, e:e + 1])
                    if c < 6:
                        link(ins)
                ins.then_inc(S["br_used"], 1)
                dve.wait_ge(S["br_used"], e + 1)
            ch.inc(dve.memset(route[:, NE, :], 0.0))
            col = lambda k: route[:, 0:NE, k:k + 1].rearrange("p a b -> p (a b)")
            ch.inc(dve.tensor_tensor(col(0), cnt[:, 0, :], cnt[:, 1, :], ALU.add))
            ch.inc(dve.tensor_tensor(col(1), cnt[:, 2, :], cnt[:, 3, :], ALU.add))
            link(dve.tensor_tensor(col(2), cnt[:, 4, :], cnt[:, 5, :], ALU.add))
            ch.inc(dve.tensor_tensor(col(2), col(2), cnt[:, 6, :], ALU.add))
            for tile in range(3):
                ch.inc(dve.tensor_copy(col(3 + tile), aff[:, tile, :]))
            ch.inc(dve.memset(give.rearrange("p a b -> p (a b)"), 0.0))
            link(dve.memset(xe.rearrange("p a b -> p (a b)"), 0.0))
            dve.wait_ge(S["x1_done"], 3)

            def take(who):
                for tile, cap in ((0, CAP_C), (1, CAP_S), (2, CAP_S)):
                    ins = dve.tensor_scalar(pick[:, tile, 0:cap], iota[:, 0:cap], cur[:, who, tile:tile + 1], None,
                                            ALU.is_equal)
                ins.then_inc(S["pick_done"], 1)

            def xe_copy(n):
                dve.wait_ge(S["xe_ps"], n)
                dve.tensor_copy(xe[:, 0:8, 0:48], ps[6][:, :].rearrange("p (k c) -> p k c", c=64)[:, :, 0:48])\
                   .then_inc(S["xe_d"], 1)

            link(dve.tensor_copy(cur[:, 0, :], route[:, 0, :]))
            take(0)
            xe_copy(1)
            dve.sem_inc(S["cb_used"], 1)
            per = 1
            base = ch.base + ch.n
            with dve.Fori(0, NE) as e:
                ch.base, ch.n = e * per + base, 0
                link(dve.tensor_copy(cur, route[:, bass.ds(e, 2), :]))
                take(1)
                for r0 in (0, 64):
                    for tile, c0, cap in ((0, CAP_S, CAP_C), (1, 0, CAP_S), (2, 0, CAP_S)):
                        ins = dve.tensor_scalar(give[:, tile, r0 + c0:r0 + c0 + cap], iota[:, 0:cap],
                                                cur[:, 0, tile:tile + 1], cur[:, 0, 3 + tile:4 + tile],
                                                ALU.is_equal, ALU.mult)
                ins.then_inc(S["give_done"], 1)
                dve.wait_ge(S["comb_ps"], e + 1)
                dve.tensor_copy(comb.rearrange("p a b -> p (a b)"), ps[5][:, 0:NT]).then_inc(S["comb_done"], 1)
                m = N_EXP + 7
                dve.wait_ge(S["sil_done"], e + 1)
                dve.wait_ge(used[m % RING], m // RING + 1 + e * 2)
                dve.tensor_tensor(hid, ps[1][:, :], sil, ALU.mult).then_inc(S["hid_done"], 1)
                xe_copy(e + 2)
                dve.wait_ge(S["hT_ps"], e + 1)
                dve.tensor_copy(hidT.rearrange("p a b -> p (a b)"), ps[2][:, :]).then_inc(S["hT_done"], 1)
                m = N_EXP + 11
                dve.wait_ge(used[m % RING], m // RING + 1 + e * 2)
                dve.wait_ge(ld_g2, 64)
                dve.tensor_tensor(ye[:, 0, :], ps[3][:, :], g2[:, 0, :], ALU.mult)
                dve.tensor_tensor(ye[:, 1, :], ps[4][:, :], g2[:, 1, :], ALU.mult).then_inc(S["ye_done"], 1)
                for q in range(12):
                    tile, u = q // 4, (0, 2, 1, 3)[q % 4]
                    dve.wait_ge(S["cb_ps"], e * 12 + q + 1)
                    out = acc[:, tile, u * 512:(u + 1) * 512]
                    dve.tensor_tensor(out, ps[SCATTER_BANKS[q % 6]][:, :], out, ALU.add).then_inc(S["cb_used"], 1)
                assert ch.n == per
            ch.base, ch.n = base + NE * per, 0

            dve.wait_ge(S["cb_used"], 12 * NE + 1)
            dve.wait_ge(ld_ln2, 32)
            for tile in range(3):
                normalise(tile, 4 + tile)
                link(dve.tensor_tensor(acc[:, tile, :], acc[:, tile, :], ln2[:, 0, :], ALU.mult))
                dve.tensor_tensor(acc[:, tile, :], acc[:, tile, :], ln2[:, 1, :], ALU.add)\
                   .then_inc(S["out_ready"], 1)


_INS = ["x_prompt", "x_sample", "cache_kv_c", "cache_k_rope", "c", "c_ctx", "w_ada", "b_ada", "w_in",
        "q_norm_g", "kv_norm_g", "w_uq", "w_ukv", "w_o_mla", "hy_short_w", "hy_short_b",
        "hy_filt_w1", "hy_filt_b1", "hy_filt_freq1", "hy_filt_w2", "hy_filt_b2", "hy_filt_freq2",
        "hy_filt_w3", "hy_filt_b3", "hy_skip", "w_o_hy", "w_out", "ln1_g", "ln1_b", "ln2_g", "ln2_b",
        "w_router", "w_gate", "w_up", "w_down"]
_OUTS = [((1, 128, 2048), "float32"), ((1, 256, 2048), "float32"),
         ((1, 1, 128, 256), "float32"), ((1, 1, 128, 64), "float32")]


def shape_constants():
    import numpy as np
    f32 = np.float32
    kc = np.zeros((P, 546), f32)
    kc[:, 0:128] = np.eye(P)
    for r in range(P):
        if (r // 16) % 2 == 0:
            kc[r + 16, 128 + r] = -1.0
            kc[r, 128 + r + 16] = 1.0
    kc[:, 256:384] = np.tril(np.ones((P, P)), -1)
    kc[:, 384:416] = np.arange(32)
    kc[1:, 416] = 1.0
    kc[:, 417] = 1.0
    tok = np.arange(LS)
    inv = (f32(10000.0) ** (-np.arange(16, dtype=f32) / f32(16))).astype(f32)
    ang = np.stack([(tok // 64).astype(f32)[:, None] * inv, (tok % 64).astype(f32)[:, None] * inv], axis=1)
    cos, sin = np.cos(ang).astype(f32), np.sin(ang).astype(f32)
    for j, tab in enumerate((cos, sin)):
        for tile in range(2):
            c0 = 418 + 64 * j + 32 * tile
            kc[:, c0:c0 + 32] = tab[tile * P:(tile + 1) * P].reshape(P, 32)
    rope_q = np.zeros((P, 2, LS), f32)
    for r in range(P):
        axis, f = (r % 64) // 32, r % 16
        rope_q[r, 0], rope_q[r, 1] = cos[:, axis, f], sin[:, axis, f]
    feats = np.zeros((EMB, NT), f32)
    window = np.zeros((P, 3, HY), f32)
    deltas = np.abs(np.linspace(math.log(0.01) / 1.5, math.log(0.01) / 0.3, HY, dtype=f32))
    bands = np.linspace(1e-4, 15, 16, dtype=f32)
    for L, a, blocks in ((LC, 0, (0,)), (LS, LC, (1, 2))):
        pos = np.arange(L, dtype=f32)
        tt = pos / f32(L - 1)
        w = f32(2.0 * math.pi) * pos / f32(L)
        wb = w[:, None] * bands
        feats[:, a:a + L] = np.concatenate([tt[:, None], np.cos(wb), -np.sin(wb)], axis=-1).T
        win = np.exp(-tt[:, None] * deltas)
        for i, blk in enumerate(blocks):
            window[:, blk] = win[i * P:(i + 1) * P]
    dft = np.zeros((P, 2560), f32)
    for L, f0, i0 in ((LS, 0, 1280), (LC, 1024, 2304)):
        n = L // P
        x = np.pi * (np.arange(L) + 0.5)[None, :] * np.arange(L)[:, None] / L
        for j, tab in enumerate((np.cos(x), np.sin(x))):
            for blk in range(n):
                c0 = j * n * L + blk * L
                dft[:, f0 + c0:f0 + c0 + L] = tab[blk * P:(blk + 1) * P]
                dft[:, i0 + c0:i0 + c0 + L] = tab.T[blk * P:(blk + 1) * P] / L
    return {"kconst": kc, "rope_q": rope_q, "feats": feats, "window": window, "dft": dft}


def kernel(**inputs):
    import numpy as _np
    import concourse.bacc as _bacc
    from concourse import mybir as _mybir
    from concourse.bass_utils import run_bass_kernel_spmd as _run

    nc = _bacc.Bacc("TRN2", target_bir_lowering=False, num_devices=1)
    arrays, tensors, consts = {}, {}, {}

    def declare(name, a, into):
        arrays[f"in_{name}_dram"] = a
        into[name] = nc.dram_tensor(f"in_{name}_dram", a.shape, _mybir.dt.from_np(a.dtype), kind="ExternalInput").ap()

    for name in _INS:
        declare(name, _np.ascontiguousarray(inputs[name]), tensors)
    for name, a in shape_constants().items():
        declare(name, a, consts)
    outs = [nc.dram_tensor(f"out_{i}_dram", shape, _mybir.dt.from_np(_np.dtype(dtype)), kind="ExternalOutput").ap()
            for i, (shape, dtype) in enumerate(_OUTS)]
    mods_dram = nc.dram_tensor("mods_dram", (4, 2, D), F32, kind="Internal").ap()
    build(nc, tensors, consts, outs, mods_dram)
    r = _run(nc, [arrays], core_ids=[0])
    return tuple(r.results[0][f"out_{i}_dram"] for i in range(len(_OUTS)))
```
